# Optimizing a Trainium2 kernel written in Bass

```python
import jax, jax.numpy as jnp
from jax import lax
import numpy as np

D_MODEL = 1024
BATCH = 1
SEQ = 256
DEPTH = 2

N_HEADS = 16
HEAD_DIM = D_MODEL // N_HEADS
N_MIXERS = 2
DILATED_GROUPS = ((128, 1), (512, 4), (2048, 16))
N_DIL_GROUPS = len(DILATED_GROUPS)
N_KV_HEADS = 4
Q_PER_KV = N_HEADS // N_KV_HEADS
Q_BLOCK = 128
GRID_W = 64
ROPE_THETA = 10000.0
D_FF = (7 * D_MODEL) // 2
N_EXPERTS = 8
TOP_K = 2
N_MOD = 6
EPS = 1e-6
NEG_INF = -1e30

kernel_name = 'hybrid_dilated_axial_moe_encoder'

def rms_norm(x, g):
    xf = x.astype(jnp.float32)
    y = xf * lax.rsqrt(jnp.mean(xf * xf, axis=-1, keepdims=True) + EPS)
    return (y * g.astype(jnp.float32)).astype(x.dtype)

def modulate(x, g, shift, scale):
    return rms_norm(x, g) * (1 + scale[:, None, :]) + shift[:, None, :]

def alibi_slopes(n):
    return jnp.exp2(-8.0 * jnp.arange(1, n + 1, dtype=jnp.float32) / n)

def dilated_window_attention(q, k, v, window, dilation, slopes):
    B, T, H, dh = q.shape
    n_side = window // (2 * dilation)
    blk = n_side
    L = T // dilation
    nb = -(-L // blk)
    Lp = nb * blk

    def split(a):
        a = a.reshape(B, L, dilation, H, dh).transpose(0, 2, 3, 1, 4)
        return jnp.pad(a, ((0, 0), (0, 0), (0, 0), (0, Lp - L), (0, 0)))

    def band(a):
        ap = jnp.pad(a, ((0, 0), (0, 0), (0, 0), (blk, blk), (0, 0)))
        ap = ap.reshape(B, dilation, H, nb + 2, blk, dh)
        return jnp.concatenate([ap[:, :, :, :-2], ap[:, :, :, 1:-1], ap[:, :, :, 2:]], axis=4)

    qb = split(q).reshape(B, dilation, H, nb, blk, dh)
    kb = band(split(k))
    vb = band(split(v))
    a = jnp.arange(blk)
    b = jnp.arange(3 * blk)
    i = jnp.arange(nb)
    rel = b[None, :] - blk - a[:, None]
    u_key = (i[:, None] - 1) * blk + b[None, :]
    valid = (jnp.abs(rel) <= n_side)[None] & ((u_key >= 0) & (u_key < L))[:, None, :]
    bias = -slopes[:, None, None] * (dilation * jnp.abs(rel)).astype(jnp.float32)
    s = jnp.einsum('brhnqd,brhnkd->brhnqk', qb, kb, preferred_element_type=jnp.float32) * (dh ** -0.5)
    s = jnp.where(valid, s + bias[:, None], NEG_INF)
    m = jnp.max(s, axis=-1, keepdims=True)
    p = jnp.exp(s - m)
    den = jnp.sum(p, axis=-1)
    o = jnp.einsum('brhnqk,brhnkd->brhnqd', p.astype(vb.dtype), vb,
                   preferred_element_type=jnp.float32) / den[..., None]
    lse = m[..., 0] + jnp.log(den)
    o = o.reshape(B, dilation, H, Lp, dh)[:, :, :, :L].transpose(0, 3, 1, 2, 4).reshape(B, T, H, dh)
    lse = lse.reshape(B, dilation, H, Lp)[:, :, :, :L].transpose(0, 3, 1, 2).reshape(B, T, H)
    return o, lse

def dilated_mixer(h, w_in, w_out):
    B, T, D = h.shape
    slopes = alibi_slopes(N_HEADS)
    outs, lses = [], []
    for g, (window, dilation) in enumerate(DILATED_GROUPS):
        qkv = (h @ w_in[:, g * 3 * D:(g + 1) * 3 * D]).reshape(B, T, 3, N_HEADS, HEAD_DIM)
        o, lse = dilated_window_attention(qkv[:, :, 0], qkv[:, :, 1], qkv[:, :, 2], window, dilation, slopes)
        outs.append(o)
        lses.append(lse)
    wts = jax.nn.softmax(jnp.stack(lses, axis=0), axis=0)
    o = jnp.sum(wts[..., None] * jnp.stack(outs, axis=0), axis=0)
    return o.reshape(B, T, D).astype(h.dtype) @ w_out

def rope_1d(x, pos):
    half = x.shape[-1] // 2
    freqs = ROPE_THETA ** (-jnp.arange(half, dtype=jnp.float32) / half)
    ang = pos[:, None] * freqs[None, :]
    cos = jnp.cos(ang)[None, :, None, :]
    sin = jnp.sin(ang)[None, :, None, :]
    x1, x2 = x[..., :half], x[..., half:]
    return jnp.concatenate([x1 * cos - x2 * sin, x1 * sin + x2 * cos], axis=-1)

def axial_rope(x):
    B, T, H, dh = x.shape
    rows = T // GRID_W
    row = jnp.broadcast_to(jnp.arange(rows, dtype=jnp.float32)[:, None], (rows, GRID_W)).reshape(T)
    col = jnp.broadcast_to(jnp.arange(GRID_W, dtype=jnp.float32)[None, :], (rows, GRID_W)).reshape(T)
    xf = x.astype(jnp.float32)
    r = dh // 2
    return jnp.concatenate([rope_1d(xf[..., :r], row), rope_1d(xf[..., r:], col)], axis=-1).astype(x.dtype)

def axial_gqa_mixer(h, w_in, q_norm_g, k_norm_g, w_out):
    B, T, D = h.shape
    kv_w = N_KV_HEADS * HEAD_DIM
    proj = h @ w_in
    q = proj[..., :D].reshape(B, T, N_HEADS, HEAD_DIM)
    k = proj[..., D:D + kv_w].reshape(B, T, N_KV_HEADS, HEAD_DIM)
    v = proj[..., D + kv_w:].reshape(B, T, N_KV_HEADS, HEAD_DIM)
    q = axial_rope(rms_norm(q, q_norm_g))
    k = axial_rope(rms_norm(k, k_norm_g))
    nq = T // Q_BLOCK
    qb = q.reshape(B, nq, Q_BLOCK, N_KV_HEADS, Q_PER_KV, HEAD_DIM).transpose(1, 0, 2, 3, 4, 5)
    scale = HEAD_DIM ** -0.5

    def attend(q_blk):
        s = jnp.einsum('bqkgd,bskd->bkgqs', q_blk, k, preferred_element_type=jnp.float32) * scale
        p = jax.nn.softmax(s, axis=-1)
        return jnp.einsum('bkgqs,bskd->bqkgd', p.astype(v.dtype), v)

    o = lax.map(attend, qb)
    o = o.transpose(1, 0, 2, 3, 4, 5).reshape(B, T, D)
    return o @ w_out

def swiglu(h, w_gate, w_up, w_down):
    return (jax.nn.silu(h @ w_gate) * (h @ w_up)) @ w_down

def moe_swiglu(h, router_w, w_gate, w_up, w_down):
    logits = (h @ router_w).astype(jnp.float32)
    top_val, top_idx = lax.top_k(logits, TOP_K)
    top_w = jax.nn.softmax(top_val, axis=-1)
    gates = jnp.sum(jax.nn.one_hot(top_idx, N_EXPERTS, dtype=jnp.float32) * top_w[..., None], axis=-2)
    gates = gates.astype(h.dtype)
    y = jnp.zeros_like(h)
    for e in range(N_EXPERTS):
        y = y + gates[..., e:e + 1] * swiglu(h, w_gate[e], w_up[e], w_down[e])
    return y

def setup_inputs(seed: int = 0) -> dict:
    key = jax.random.key(seed)
    ks = jax.random.split(key, 18)
    f32 = jnp.float32
    D = D_MODEL

    def nrm(k, shape, fan_in):
        return jax.random.normal(k, shape, f32) * (fan_in ** -0.5)

    return {
        'x': jax.random.normal(ks[0], (BATCH, SEQ, D), f32),
        'c': jax.random.normal(ks[1], (BATCH, D), f32),
        'mod_w': nrm(ks[2], (DEPTH, D, N_MOD * D), D),
        'mod_b': 0.02 * jax.random.normal(ks[3], (DEPTH, N_MOD * D), f32),
        'norm_g': 1.0 + 0.02 * jax.random.normal(ks[4], (DEPTH, 4, D), f32),
        'l0_w_in': nrm(ks[5], (D, N_DIL_GROUPS * 3 * D), D),
        'l0_w_out': nrm(ks[6], (D, D), D),
        'l0_ffn_w_gate': nrm(ks[7], (D, D_FF), D),
        'l0_ffn_w_up': nrm(ks[8], (D, D_FF), D),
        'l0_ffn_w_down': nrm(ks[9], (D_FF, D), D_FF),
        'l1_w_in': nrm(ks[10], (D, D + 2 * N_KV_HEADS * HEAD_DIM), D),
        'l1_q_norm_g': 1.0 + 0.02 * jax.random.normal(ks[11], (HEAD_DIM,), f32),
        'l1_k_norm_g': 1.0 + 0.02 * jax.random.normal(ks[12], (HEAD_DIM,), f32),
        'l1_w_out': nrm(ks[13], (D, D), D),
        'l1_router_w': nrm(ks[14], (D, N_EXPERTS), D),
        'l1_exp_w_gate': nrm(ks[15], (N_EXPERTS, D, D_FF), D),
        'l1_exp_w_up': nrm(ks[16], (N_EXPERTS, D, D_FF), D),
        'l1_exp_w_down': nrm(ks[17], (N_EXPERTS, D_FF, D), D_FF),
    }

def reference(x, c, mod_w, mod_b, norm_g, l0_w_in, l0_w_out, l0_ffn_w_gate, l0_ffn_w_up, l0_ffn_w_down,
              l1_w_in, l1_q_norm_g, l1_k_norm_g, l1_w_out, l1_router_w, l1_exp_w_gate, l1_exp_w_up,
              l1_exp_w_down):
    mixers = (
        lambda h: dilated_mixer(h, l0_w_in, l0_w_out),
        lambda h: axial_gqa_mixer(h, l1_w_in, l1_q_norm_g, l1_k_norm_g, l1_w_out),
    )
    channel_mixers = (
        lambda h: swiglu(h, l0_ffn_w_gate, l0_ffn_w_up, l0_ffn_w_down),
        lambda h: moe_swiglu(h, l1_router_w, l1_exp_w_gate, l1_exp_w_up, l1_exp_w_down),
    )
    c_act = jax.nn.silu(c)
    for i in range(DEPTH):
        mod = c_act @ mod_w[i] + mod_b[i]
        sh_a, sc_a, g_a, sh_f, sc_f, g_f = jnp.split(mod, N_MOD, axis=-1)
        y = mixers[i % N_MIXERS](modulate(x, norm_g[i, 0], sh_a, sc_a))
        x = x + g_a[:, None, :] * rms_norm(y, norm_g[i, 1])
        y = channel_mixers[i % 2](modulate(x, norm_g[i, 2], sh_f, sc_f))
        x = x + g_f[:, None, :] * rms_norm(y, norm_g[i, 3])
    return x


_drawn_inputs = setup_inputs


def setup_inputs(seed=0):
    import zlib

    import numpy as np

    out = dict(_drawn_inputs(seed))
    spreads = {}
    factors = {'l1_q_norm_g': 3.654, 'l1_k_norm_g': 3.653}
    for name, (base, spread) in spreads.items():
        noise = np.random.default_rng([zlib.crc32(name.encode()), seed]).standard_normal(out[name].shape)
        drawn = base * np.exp(spread * noise) if base else spread * noise
        out[name] = __import__('jax').numpy.asarray(drawn.astype(out[name].dtype))
    for name, factor in factors.items():
        out[name] = (out[name] * factor).astype(out[name].dtype)
    return out
```

```python
from contextlib import ExitStack

import numpy as np
import concourse.bass as bass
from concourse import mybir

F32 = mybir.dt.float32
F32R = mybir.dt.float32r
BF16 = mybir.dt.bfloat16
I32 = mybir.dt.int32
ALU = mybir.AluOpType
ACT = mybir.ActivationFunctionType
AX = mybir.AxisListType.X

DGE_RING = 3072
VECTORS = 4 * 16
SETUP = 4 * 16
R_CHOSEN = 13
R_DIFF = 14
ROPE_TILE = 7
ROPE_END = 1 + 5 * ROPE_TILE

P = 128
D = 1024
T = 256
NT = T // P
KC = D // P
NH = 16
DH = D // NH
NKV = 4
NG = 3
DILATIONS = (1, 4, 16)
SIDE = 64
FF = 3584
NE = 8
NEXTRA = 3
NPASS = NE + NEXTRA
GRID_W = 64
EPS = 1e-6
BIG = 1e30
BANK = 512

RAW = 6
SPL = 3
MRAW = 4
TILE = 2048

M_QKV = 0
N_QKV_HALF = NG * 3 * 2
M_WO0 = M_QKV + 2 * N_QKV_HALF
M_FFN = M_WO0 + 4
NHALF = FF // 256
M_IN1 = M_FFN + 3 * NHALF
N_IN1 = 6
V_FFN = 8
M_WO1 = M_IN1 + N_IN1
M_MOE = M_WO1 + 4
NF = FF // 512
N_PASS = 6 * NF
SCATTER_BANKS = (2, 3, 7, 5)

C_ID, C_ONE, C_UP, C_IOTA, C_DESC, C_EI, C_COS, C_SIN, C_DIST = 0, 128, 256, 384, 512, 520, 528, 656, 784
NCONST = C_DIST + NT * NG * T


def constants():
    c = np.zeros((P, NCONST), np.float32)
    c[:, C_ID:C_ID + P] = np.eye(P)
    c[:, C_ONE:C_ONE + P] = 1.0
    c[:, C_UP:C_UP + P] = np.triu(np.ones((P, P)), 1)
    c[:, C_IOTA:C_IOTA + P] = np.arange(P)
    c[:, C_DESC:C_DESC + NE] = NE - np.arange(NE)
    c[:, C_EI:C_EI + NE] = np.arange(NE)
    q = DH // 4
    freq = (np.float32(10000.0) ** (-np.arange(q, dtype=np.float32) / q)).astype(np.float32)
    for tt in range(NT):
        t = tt * P + np.arange(P)
        for n, pos in enumerate((t // GRID_W, t % GRID_W)):
            ang = pos.astype(np.float32)[:, None] * freq[None]
            at = C_COS + tt * DH + n * 2 * q
            c[:, at:at + q] = c[:, at + q:at + 2 * q] = np.cos(ang)
            at = C_SIN + tt * DH + n * 2 * q
            c[:, at:at + q] = -np.sin(ang)
            c[:, at + q:at + 2 * q] = np.sin(ang)
        dist = np.abs(t[:, None] - np.arange(T)[None]).astype(np.float32)
        for g, dil in enumerate(DILATIONS):
            seen = (dist % dil == 0) & (dist <= SIDE * dil)
            at = C_DIST + (tt * NG + g) * T
            c[:, at:at + T] = 16 * np.where(seen, dist, np.float32(BIG))
    return c


def slope(h):
    return float(np.exp2(np.float32(-8.0 * (h + 1) / NH)))


def build(nc, dram, out):
    ctx = ExitStack()
    with ctx:
        def sb(name, shape, dt=F32):
            return ctx.enter_context(nc.sbuf_tensor(name, shape, dt))

        def sem(name):
            return ctx.enter_context(nc.semaphore(name))

        raw = [sb(f"raw{i}", [P, TILE]) for i in range(RAW)]
        whi = [sb(f"whi{i}", [P, TILE], F32R) for i in range(SPL)]
        wlo = [sb(f"wlo{i}", [P, TILE], F32R) for i in range(SPL)]
        mraw = [sb(f"mraw{i}", [P, D]) for i in range(MRAW)]
        acc = sb("acc", [P, D])
        xs = sb("xs", [P, NT, D])
        xo = sb("xo", [P, NT, D])
        oT = xo[:, :, :].rearrange("p a (b t) -> p (a b) t", t=T)
        ahi = sb("ahi", [P, KC, T], F32R)
        alo = sb("alo", [P, KC, T], F32R)
        gb = sb("gb", [P, D])
        cst = sb("cst", [P, NCONST])
        vcol = sb("vcol", [P, 72])
        bcol = sb("bcol", [P, 96])
        ccol = sb("ccol", [P, KC])
        mcol = sb("mcol", [P, 12, KC])
        acol = sb("acol", [P, 4, KC])
        gcol = sb("gcol", [P, 4, KC])
        ss = sb("ss", [P, 8, NT])
        rms = sb("rms", [P, 8, NT])
        rstd = sb("rstd", [P, 8, NT])
        gq = sb("gq", [P, 2, DH])
        zb = sb("zb", [P, BANK], BF16)
        arena = sb("arena", [P, 13056])
        rows = arena[:, 11776:12032].rearrange("p (a c) -> p a c", a=2)
        ht = arena[:, 0:KC * T].rearrange("p (k t) -> p k t", k=KC)
        dg = arena[:, 2048:3072]
        QT = arena[:, 0:3072].rearrange("p (g j t) -> p g j t", g=NG, j=4)
        KT = arena[:, 3072:6144].rearrange("p (g j t) -> p g j t", g=NG, j=4)
        V0 = arena[:, 6144:9216].rearrange("p (t g c) -> p t g c", t=NT, g=NG)
        SB = arena[:, 9216:11520].rearrange("p (b k) -> p b k", b=3)
        PT = arena[:, 11520:13056].rearrange("p (b k) -> p b k", b=2)
        qkv = arena[:, 0:3072].rearrange("p (t c) -> p t c", t=NT)
        t1 = arena[:, 3072:6144].rearrange("p (t c) -> p t c", t=NT)
        t2 = arena[:, 9216:10240].rearrange("p (n t h d) -> p n t h d", n=2, t=NT, d=DH)
        QT1 = arena[:, 6144:8192].rearrange("p (j t) -> p j t", j=KC)
        KT1 = arena[:, 8192:9216].rearrange("p (j t) -> p j t", j=NKV)
        P1 = arena[:, 9216:10752].rearrange("p (b k) -> p b k", b=3)
        PT1 = arena[:, 10752:11776].rearrange("p (b k) -> p b k", b=2)
        cg = arena[:, 12288:12544].rearrange("p (t n d) -> p t n d", t=NT, n=2)
        sg_ = arena[:, 12544:12800].rearrange("p (t n d) -> p t n d", t=NT, n=2)
        hs1 = arena[:, 12800:12920].rearrange("p (n k t h) -> p n k t h", n=3, k=5, t=NT)
        sgl = arena[:, 3072:3584]
        hsb = arena[:, 3584:4096]
        hhi = sb("hhi", [P, BANK], F32R)
        hlo = sb("hlo", [P, BANK], F32R)
        yacc = arena[:, 4096:6144].rearrange("p (t c) -> p t c", t=NT)
        ye = arena[:, 6144:7168]
        xg = arena[:, 7168:8192].rearrange("p (k t) -> p k t", k=KC)
        Sel = arena[:, 8192:8448].rearrange("p (t s) -> p t s", t=NT)
        Sg = arena[:, 8448:8704].rearrange("p (t s) -> p t s", t=NT)
        SgT = arena[:, 8704:8960]
        rt = arena[:, 8960:9600]
        rw = sb("rw", [P, KC, NE])
        tab = sb("tab", [P, NPASS + 1, 4])
        cur = sb("cur", [P, 8])
        warm = sb("warm", [P, 1])
        idf = sb("idf", [P, 16])
        ids = sb("ids", [1, 16], I32)
        nm = sb("nm", [P, 32])
        den = sb("den", [P, 32])
        rden = sb("rden", [P, 32])
        R = {name: 16 * n for n, name in enumerate((
            "L", "eq", "cand", "oh1", "l2", "oh2", "mask", "gate", "rank", "tmp", "tmp2", "gt2", "pair"))}
        R_S = 16 * len(R)
        R_M1, R_F, R_M2, R_D, R_E, R_G1, R_G2, R_F2 = (R_S + 2 * n for n in range(8))
        R_OVF = R_S + 16
        R_CUM = R_S + 24

        ident = cst[:, C_ID:C_ID + P]
        ones = cst[:, C_ONE:C_ONE + P]
        upper = cst[:, C_UP:C_UP + P]
        iota = cst[:, C_IOTA:C_IOTA + P]

        ps = ctx.enter_context(nc.psum_tensor("ps", [P, 8 * BANK], F32))

        def bank(b, a=0, z=BANK):
            return ps[:, b * BANK + a:b * BANK + z]

        vectors = sem("vectors")
        setup = sem("setup")
        dist_landed = sem("dist_landed")
        zeroed = sem("zeroed")
        landed = [sem(f"landed{i}") for i in range(RAW)]
        hi_done = sem("hi_done")
        lo_done = sem("lo_done")
        w_used = sem("w_used")
        mod_landed = [sem(f"mod_landed{i}") for i in range(MRAW)]
        mod_used = sem("mod_used")
        colsum = sem("colsum")
        mcol_done = sem("mcol_done")
        turned = sem("turned")
        cols = sem("cols")
        c_act = sem("c_act")
        sq_done = sem("sq_done")
        rs_done = sem("rs_done")
        sqrt_done = sem("sqrt_done")
        hroot = sem("hroot")
        acol_done = sem("acol_done")
        xn_done = sem("xn_done")
        xT_done = sem("xT_done")
        ht_done = sem("ht_done")
        htv_done = sem("htv_done")
        first_out = sem("first_out")
        ahi_done = sem("ahi_done")
        alo_done = sem("alo_done")
        gcol_done = sem("gcol_done")
        dg_done = sem("dg_done")
        gbp_done = sem("gbp_done")
        gb_done = sem("gb_done")
        post_t = sem("post_t")
        x_new = sem("x_new")
        qkv_evac = sem("qkv_evac")
        s_done = sem("s_done")
        sb_done = sem("sb_done")
        nm_done = sem("nm_done")
        e_done = sem("e_done")
        pt_done = sem("pt_done")
        pte_a = sem("pte_a")
        pte_v = sem("pte_v")
        pv_done = sem("pv_done")
        rd_done = sem("rd_done")
        pn_done = sem("pn_done")
        o_done = sem("o_done")
        dist_ok = sem("dist_ok")
        silu_done = sem("silu_done")
        h_ready = sem("h_ready")
        t_done = sem("t_done")
        hhi_done = sem("hhi_done")
        hlo_done = sem("hlo_done")
        in1_evac = sem("in1_evac")
        rope = sem("rope")
        q1_evac = sem("q1_evac")
        logits = sem("logits")
        route = sem("route")
        e_gate = sem("e_gate")
        counted = sem("counted")
        routed = sem("routed")
        sel_done = sem("sel_done")
        sg_done = sem("sg_done")
        cur_done = sem("cur_done")
        selT = sem("selT")
        selT_e = sem("selT_e")
        gath = sem("gath")
        xg_done = sem("xg_done")
        ye_done = sem("ye_done")
        scat = sem("scat")
        y_add = sem("y_add")
        stored = sem("stored")

        block = ctx.enter_context(nc.Block())

        def shift_of(k):
            return mcol[:, (k // 2) * 6 + (k % 2) * 3, :]

        def scale_of(k):
            return mcol[:, (k // 2) * 6 + (k % 2) * 3 + 1, :]

        def gate_of(k):
            return mcol[:, (k // 2) * 6 + (k % 2) * 3 + 2, :]

        def norm_of(k, post):
            at = ((k // 2) * 4 + (k % 2) * 2 + post) * KC
            return vcol[:, at:at + KC]

        def waits(eng, s, value):
            if not isinstance(value, int) or value > 0:
                eng.wait_ge(s, value)

        @block.sync
        def _(sp):
            def fetch(s, rr, src, dims):
                waits(sp, lo_done, s - RAW + 1 + 6 * rr)
                k, n = dims
                sp.dma_start(raw[s % RAW][:, :].rearrange("p (k n) -> p k n", k=k), src).then_inc(landed[s % RAW], 16)

            def columns(w, c0, n=256):
                return w[:, bass.ds(c0, n)].rearrange("(k p) c -> p k c", p=P)

            def rows_of(w, r0, n=256):
                return w[bass.ds(r0, n), :].rearrange("(k p) c -> p k c", p=P)

            w_in = dram["l0_w_in"]

            def qkv_group(half, g, rr):
                for n in range(3):
                    for c in range(2):
                        fetch(M_QKV + n * 2 + c, rr, columns(w_in, half * 512 + g * 3 * D + n * D + c * 256),
                              (KC, 256))

            sp.wait_ge(mod_used, 13)
            qkv_group(0, 0, 0)
            sp.dma_start(cst[:, C_DIST:NCONST], dram["consts"][:, C_DIST:NCONST]).then_inc(dist_landed, 16)
            with sp.Fori(1, NG) as g:
                qkv_group(0, g, g)
            with sp.Fori(0, NG) as g:
                qkv_group(1, g, g + NG)
            for k in range(4):
                fetch(M_WO0 + k, 0, rows_of(dram["l0_w_out"], 256 * k), (2, D))

            def gate_up(h, s, rr):
                fetch(s, rr, columns(dram["l0_ffn_w_gate"], h * 256), (KC, 256))
                fetch(s + 1, rr, columns(dram["l0_ffn_w_up"], h * 256), (KC, 256))

            def down(h, s, rr):
                fetch(s, rr, rows_of(dram["l0_ffn_w_down"], h * 256), (2, D))

            gate_up(0, M_FFN, 0)
            with sp.Fori(0, (NHALF - 2) // 2) as i:
                for k in range(2):
                    gate_up(2 * i + k + 1, M_FFN + 2 + 3 * k, i)
                    down(2 * i + k, M_FFN + 4 + 3 * k, i)
            gate_up(NHALF - 1, M_FFN + 3 * NHALF - 4, 0)
            down(NHALF - 2, M_FFN + 3 * NHALF - 2, 0)
            down(NHALF - 1, M_FFN + 3 * NHALF - 1, 0)
            for k in range(N_IN1):
                fetch(M_IN1 + k, 0, columns(dram["l1_w_in"], 256 * k), (KC, 256))
            for k in range(4):
                fetch(M_WO1 + k, 0, rows_of(dram["l1_w_out"], 256 * k), (2, D))

            def expert_half(name, e, k, c0):
                return dram[name][bass.ds(e, 1), 512 * k:512 * k + 512, bass.ds(c0, 512)].rearrange(
                    "a (k p) c -> p (a k) c", p=P)

            def e_gate_up(e, i, s, rr):
                for w, name in enumerate(("l1_exp_w_gate", "l1_exp_w_up")):
                    for k in range(2):
                        fetch(s + 2 * w + k, rr, expert_half(name, e, k, i * 512), (4, 512))

            def e_down(e, i, s, rr):
                for k in range(2):
                    fetch(s + k, rr, dram["l1_exp_w_down"][bass.ds(e, 1), bass.ds(i * 512 + 256 * k, 256), :]
                          .rearrange("a (k p) c -> p (a k) c", p=P), (2, D))

            def expert_pass(e, rr):
                e_gate_up(e, 0, M_MOE, rr)
                with sp.Fori(1, NF) as i:
                    e_gate_up(e, i, M_MOE + 4, rr + i - 1)
                    e_down(e, i - 1, M_MOE + 8, rr + i - 1)
                e_down(e, NF - 1, M_MOE + N_PASS - 2, rr)

            expert_pass(0, 0)
            sp.wait_ge(routed, 1)
            npass = sp.value_load(ids[0:1, NPASS + 1:NPASS + 2], min_val=NE, max_val=NPASS)
            with sp.Fori(1, npass) as p:
                e = sp.value_load(ids[0:1, bass.ds(p, 1)], min_val=0, max_val=NE - 1)
                expert_pass(e, NF * p)
            for k in range(SPL):
                fetch(M_MOE + k, NF * npass, expert_half("l1_exp_w_gate", 0, 0, 0), (4, 512))
            sp.wait_ge(x_new, 8)
            sp.dma_start(out.rearrange("b (t p) d -> p (b t) d", p=P), xs[:, :, :]).then_inc(stored, 16)
            sp.wait_ge(stored, 16)

        @block.gpsimd
        def _(pool):
            def fetch_vector(layer, v):
                for kc in range(KC):
                    waits(pool, mod_used, 48 * layer + 8 * v + kc - MRAW + 1)
                    src = dram["mod_w"][layer, kc * P:(kc + 1) * P, bass.ds(v * D, D)]
                    pool.dma_start(mraw[kc % MRAW][:, :], src).then_inc(mod_landed[kc % MRAW], 16)

            fetch_vector(0, 0)
            with pool.Fori(1, 6) as v:
                fetch_vector(0, v)
            with pool.Fori(0, 6) as v:
                fetch_vector(1, v)

        @block.scalar
        def _(act):
            def high(s, rr=0):
                act.wait_ge(landed[s % RAW], 16 * (s // RAW + 1) + 16 * rr)
                waits(act, w_used, s - SPL + 1 + 6 * rr)
                act.activation(whi[s % SPL][:, :], raw[s % RAW][:, :], ACT.Copy).then_inc(hi_done, 1)

            def squares(c, srcs, wait_for=None):
                act.activation(warm[:, :], ones[:, 0:1], ACT.Sqrt)
                for tt in range(NT):
                    if wait_for:
                        act.wait_ge(*wait_for[tt])
                    act.activation(xo[:, tt, :], srcs[tt], ACT.Square,
                                   accum_out=ss[:, c, tt:tt + 1]).then_inc(sq_done, 1)
                act.wait_ge(rs_done, 2 * c + 1)
                act.activation(rstd[:, c, :], rms[:, c, :], ACT.Sqrt).then_inc(sqrt_done, 1)

            def modulated(k, split=True):
                act.wait_ge(acol_done, k + 1)
                for q in range(2):
                    act.wait_ge(xT_done, 4 * k + q + 1)
                    for j in range(2):
                        kc = 2 * q + j
                        ins = act.activation(ht[:, kc, :], bank(4 + q % 2, j * T, j * T + T), ACT.Identity,
                                             bias=shift_of(k)[:, kc:kc + 1], scale=acol[:, k, kc:kc + 1])
                    ins.then_inc(ht_done, 1)
                if split:
                    for q in range(4):
                        if q < 2:
                            act.wait_ge(ht_done, 2 * k + q + 1)
                        else:
                            act.wait_ge(htv_done, 2 * k + q - 1)
                        act.activation(ahi[:, 2 * q:2 * q + 2, :], ht[:, 2 * q:2 * q + 2, :],
                                       ACT.Copy).then_inc(ahi_done, 1)

            def gate_row(k):
                act.wait_ge(gbp_done, k + 1)
                act.activation(gb[:, :], ps[:, 4 * BANK:6 * BANK], ACT.Copy).then_inc(gb_done, 1)

            act.dma_start(rows[0:64, 0, :], dram["norm_g"].rearrange("l n (k p) -> (l n k) p", p=P)).then_inc(vectors, 16)
            act.dma_start(rows[64:72, 0, :], dram["c"].rearrange("b (k p) -> (b k) p", p=P)).then_inc(vectors, 16)
            act.dma_start(rows[0:96, 1, :], dram["mod_b"].rearrange("l (k p) -> (l k) p", p=P)).then_inc(vectors, 16)
            act.dma_start(cst[:, 0:C_DIST], dram["consts"][:, 0:C_DIST]).then_inc(vectors, 16)
            act.dma_start(xs[:, :, :], dram["x"].rearrange("b (t p) d -> p (b t) d", p=P)).then_inc(setup, 16)
            for n, name in enumerate(("l1_q_norm_g", "l1_k_norm_g")):
                act.dma_start(gq[:, n, :], dram[name].rearrange("(a d) -> a d", a=1).broadcast_to([P, DH]))\
                   .then_inc(setup, 16)
            act.dma_start(rw[:, :, :], dram["l1_router_w"].rearrange("(k p) e -> p k e", p=P)).then_inc(setup, 16)
            act.wait_ge(cols, 1)
            act.activation(ccol[:, :], vcol[:, 64:72], ACT.Silu).then_inc(c_act, 1)
            act.wait_ge(setup, SETUP)
            squares(0, [xs[:, tt, :] for tt in range(NT)])
            for s in range(SPL):
                high(s)
            modulated(0)

            with act.Fori(0, 2) as half:
                for k in range(N_QKV_HALF):
                    g, n, c = k // 6, k // 2 % 3, k % 2
                    act.wait_ge(w_used, k + 1 + N_QKV_HALF * half)
                    src = bank(k % 2)
                    if n == 0:
                        ins = act.activation(QT[:, g, 2 * c:2 * c + 2, :], src, ACT.Copy, scale=float(DH) ** -0.5)
                    elif n == 1:
                        ins = act.activation(KT[:, g, 2 * c:2 * c + 2, :], src, ACT.Copy)
                    else:
                        ins = act.activation(V0[:, :, g, c * 256:c * 256 + 256], src.rearrange("p (t c) -> p t c", t=NT),
                                             ACT.Copy)
                    ins.then_inc(qkv_evac, 1)
                    high(k + SPL, 3 * half)
                for t in range(20):
                    if t < 16:
                        act.wait_ge(nm_done, 16 * half + t + 1)
                        act.activation(SB[:, t % 3, :], SB[:, t % 3, :], ACT.Exp, bias=nm[:, t:t + 1],
                                       accum_out=den[:, t:t + 1]).then_inc(e_done, 1)
                    if 2 <= t <= 17:
                        u = t - 2
                        act.wait_ge(pt_done, 16 * half + u + 1)
                        act.activation(PT[:, u % 2, 0:BANK], bank(4), ACT.Copy).then_inc(pte_a, 1)
                    if t >= 7 and t % 4 == 3:
                        jp = t // 4 - 1
                        act.wait_ge(pv_done, 16 * half + 4 * jp + 4)
                        act.activation(oT[:, bass.ds(half * 4 + jp, 1), :].rearrange("p a t -> p (a t)"),
                                       bank(6 + jp % 2, 0, T), ACT.Copy).then_inc(o_done, 1)

            def mixer_out(at, m, sub, pairs):
                for q in range(4):
                    act.wait_ge(o_done, pairs - 6 + 2 * q)
                    act.activation(ahi[:, 2 * q:2 * q + 2, :], oT[:, 2 * q:2 * q + 2, :],
                                   ACT.Copy).then_inc(ahi_done, 1)
                for j in range(3):
                    high(m + j + SPL)
                gate_row(sub)
                squares_out(1 + 4 * (sub // 2), sub, m + 4)
                high(m + 3 + SPL)

            def squares_out(c, sub, used):
                squares(c, [ps[:, 2 * tt * BANK:2 * (tt + 1) * BANK] for tt in range(NT)],
                        [(first_out, sub + 1), (w_used, used)])

            def before_channel(sub):
                squares(2 + 2 * sub, [xs[:, tt, :] for tt in range(NT)], [(x_new, 2 * sub + tt + 1) for tt in range(NT)])

            mixer_out(1, M_WO0, 0, 8)
            before_channel(0)
            modulated(1)

            def silu(f, used):
                act.wait_ge(w_used, used)
                waits(act, h_ready, f)
                act.activation(sgl, bank(4), ACT.Silu).then_inc(silu_done, 1)

            def hidden_high(f):
                act.wait_ge(t_done, f + 1)
                act.activation(hhi[:, :], bank(6), ACT.Copy).then_inc(hhi_done, 1)

            def dense_step(f, s, rr):
                silu(f, s + 1 + 6 * rr)
                high(s + SPL, rr)
                hidden_high(f - 1)
                high(s + 1 + SPL, rr)
                high(s + 2 + SPL, rr)

            silu(0, M_FFN + 1)
            high(M_FFN + SPL)
            high(M_FFN + 1 + SPL)
            with act.Fori(0, (NHALF - 2) // 4) as i:
                for k in range(4):
                    dense_step(4 * i + k + 1, M_FFN + 2 + 3 * k, 2 * i)
            dense_step(NHALF - 1, M_FFN + 3 * NHALF - 4, 0)
            hidden_high(NHALF - 1)
            gate_row(1)
            squares_out(3, 1, M_IN1)
            high(M_IN1 - 1 + SPL)
            before_channel(1)
            modulated(2)

            for k in range(N_IN1):
                act.wait_ge(w_used, M_IN1 + k + 1)
                if k < 5:
                    if k:
                        act.wait_ge(rope, 2 + (k - 1) * ROPE_TILE)
                    act.activation(t2[:, 0].rearrange("p t h d -> p (t h d)"), bank(k % 2), ACT.Square)
                act.activation(qkv[:, :, k * 256:k * 256 + 256], bank(k % 2).rearrange("p (t c) -> p t c", t=NT),
                               ACT.Copy).then_inc(in1_evac, 1)
                high(M_IN1 + k + SPL)
                if k < 5:
                    act.wait_ge(rope, 3 + k * ROPE_TILE)
                    act.activation(hs1[:, 0, k], hs1[:, 1, k], ACT.Sqrt).then_inc(hroot, 1)
            for q in range(6):
                act.wait_ge(pt_done, 32 + q + 1)
                src = bank(4 + q % 2)
                if q < 4:
                    ins = act.activation(QT1[:, 2 * q:2 * q + 2, :], src, ACT.Copy, scale=float(DH) ** -0.5)
                else:
                    ins = act.activation(KT1[:, 2 * q - 8:2 * q - 6, :], src, ACT.Copy)
                ins.then_inc(q1_evac, 1)
            for t in range(20):
                if t < 16:
                    u = t
                    act.wait_ge(nm_done, 32 + u + 1)
                    for r in range(2):
                        ins = act.activation(P1[:, u % 3, r * T:r * T + T], bank(2 * (u % 2) + r, 0, T), ACT.Exp,
                                             bias=nm[:, 2 * u + r:2 * u + r + 1],
                                             accum_out=den[:, 2 * u + r:2 * u + r + 1])
                    ins.then_inc(e_done, 1)
                if t >= 5 and t % 2:
                    i = (t - 5) // 2
                    act.wait_ge(pv_done, 32 + 2 * i + 2)
                    act.activation(oT[:, i, :], bank(6 + i % 2, 0, T), ACT.Copy).then_inc(o_done, 1)
            mixer_out(4, M_WO1, 2, 16)
            before_channel(2)
            modulated(3, split=False)

            act.wait_ge(route, R_DIFF)
            act.activation(rt[:, R_E:R_E + 2], rt[:, R_D:R_D + 2], ACT.Exp).then_inc(e_gate, 1)

            def gathered(p):
                for kc in range(KC):
                    if kc % 4 == 0:
                        act.wait_ge(gath, 2 * p + kc // 4 + 1)
                    ins = act.activation(xg[:, kc, :], ps[:, 2 * BANK + kc * P:2 * BANK + (kc + 1) * P], ACT.Identity,
                                         bias=shift_of(3)[:, kc:kc + 1], scale=acol[:, 3, kc:kc + 1])
                ins.then_inc(xg_done, 1)

            def gathered_high(p):
                act.wait_ge(xg_done, p + 1)
                act.activation(ahi[:, :, 0:P], xg, ACT.Copy).then_inc(ahi_done, 1)

            def expert_step(f, s, rr, first):
                high(s + SPL, rr)
                silu(f, s + 2 + 6 * rr)
                high(s + 1 + SPL, rr)
                if not first:
                    hidden_high(f - 1)
                for j in range(2, 4 if first else 6):
                    high(s + j + SPL, rr)

            gathered(0)
            gathered_high(0)
            act.wait_ge(routed, 1)
            npass = act.value_load(ids[0:1, NPASS + 1:NPASS + 2], min_val=NE, max_val=NPASS)
            with act.Fori(0, npass) as p:
                expert_step(NHALF + NF * p, M_MOE, NF * p, True)
                gathered(p + 1)
                with act.Fori(1, NF) as i:
                    expert_step(NHALF + NF * p + i, M_MOE + 4, NF * p + i - 1, False)
                hidden_high(NHALF + NF * p + NF - 1)
                act.wait_ge(w_used, M_MOE + N_PASS * p + N_PASS - 4)
                gathered_high(p + 1)
                for j in range(2):
                    high(M_MOE + N_PASS - 2 + j + SPL, NF * p)
                act.wait_ge(w_used, M_MOE + N_PASS * (p + 1))
                act.activation(ye, ps[:, 0:2 * BANK], ACT.Copy).then_inc(ye_done, 1)
            gate_row(3)
            act.wait_ge(y_add, 5 + 4 * npass)
            squares(7, [yacc[:, tt, :] for tt in range(NT)])

        @block.tensor
        def _(pe):
            def ready(s, rr=0):
                pe.wait_ge(lo_done, s + 1 + 6 * rr)

            def products(dst, stat, mov, start, stop):
                pe.matmul(dst, stat[0], mov[0], start=start, stop=False, skip_group_check=True)
                pe.matmul(dst, stat[0], mov[1], start=False, stop=False, skip_group_check=True)
                return pe.matmul(dst, stat[1], mov[0], start=False, stop=stop, skip_group_check=True)

            def act_T(kc, a, z):
                return ahi[:, kc, a:z], alo[:, kc, a:z]

            def weights(s, a, z):
                return whi[s % SPL][:, a:z], wlo[s % SPL][:, a:z]

            def tokens_by_columns(b, s, rr=0, stage=None):
                ready(s, rr)
                for tt in range(NT):
                    for kc in range(KC):
                        if stage is not None and tt == 0 and kc % 2 == 0:
                            pe.wait_ge(alo_done, 4 * stage + kc // 2 + 1)
                        ins = products(bank(b, tt * 256, tt * 256 + 256), act_T(kc, tt * P, tt * P + P),
                                       weights(s, kc * 256, kc * 256 + 256), kc == 0, kc == KC - 1)
                ins.then_inc(w_used, 1)

            def columns_by_tokens(b, s, rr=0, stage=None):
                ready(s, rr)
                for c in range(2):
                    for kc in range(KC):
                        if stage is not None and c == 0 and kc % 2 == 0:
                            pe.wait_ge(alo_done, 4 * stage + kc // 2 + 1)
                        ins = products(bank(b, c * T, c * T + T), weights(s, kc * 256 + c * P, kc * 256 + c * P + P),
                                       act_T(kc, 0, T), kc == 0, kc == KC - 1)
                ins.then_inc(w_used, 1)

            def transpose_stream(k, src_ready, after=None):
                src_ready()
                for q in range(4):
                    if q >= 2:
                        pe.wait_ge(ht_done, 2 * k + q - 1)
                        if after:
                            after(q - 2)
                    for j in range(2):
                        for tt in range(NT):
                            kc = 2 * q + j
                            ins = pe.transpose(bank(4 + q % 2, (2 * j + tt) * P, (2 * j + tt + 1) * P),
                                               xo[:, tt, kc * P:(kc + 1) * P], ident)
                    ins.then_inc(xT_done, 1)

            def column_sums(V, b=7):
                pe.wait_ge(mod_used, 8 * V + 8)
                waits(pe, mcol_done, V)
                for kc in range(KC):
                    ins = pe.matmul(bank(b, kc, kc + 1), acc[:, kc * P:(kc + 1) * P], ones[:, 0:1], start=True, stop=True)
                ins.then_inc(colsum, 1)

            def spread_gate(sub):
                pe.wait_ge(dg_done, sub + 1)
                for kc in range(KC):
                    ins = pe.matmul(ps[:, 4 * BANK + kc * P:4 * BANK + (kc + 1) * P], ones, dg[:, kc * P:(kc + 1) * P],
                                    start=True, stop=True)
                ins.then_inc(gbp_done, 1)

            pe.wait_ge(vectors, VECTORS)
            pe.transpose(bank(4, 0, 72), rows[0:72, 0, :], ident[0:72, 0:72])
            pe.transpose(bank(4, 128, 224), rows[0:96, 1, :], ident[0:96, 0:96]).then_inc(turned, 1)
            column_sums(0)
            column_sums(1)
            transpose_stream(0, lambda: (pe.wait_ge(xn_done, 2), pe.wait_ge(cols, 1)))

            with pe.Fori(0, 2) as half:
                for k in range(N_QKV_HALF):
                    if k >= 2:
                        pe.wait_ge(qkv_evac, N_QKV_HALF * half + k - 1)
                    if k // 2 % 3 < 2:
                        columns_by_tokens(k % 2, M_QKV + k, 3 * half, 0 if k == 0 else None)
                    else:
                        tokens_by_columns(k % 2, M_QKV + k, 3 * half)
                    if k == 9:
                        column_sums(3 * half + 2)
                def scores(u):
                    j, tt = u // 2, u % 2
                    r, jp = 64 * (j % 2), j // 2
                    if u == 0:
                        pe.wait_ge(qkv_evac, N_QKV_HALF * (half + 1))
                    if u >= 2:
                        pe.wait_ge(sb_done, 16 * half + u - 1)
                    for g in range(NG):
                        at = 2 * (u % 2) * BANK + g * T
                        ins = pe.matmul(ps[:, at:at + T], QT[r:r + 64, g, jp, tt * P:tt * P + P],
                                        KT[r:r + 64, g, jp, :], start=True, stop=True)
                    ins.then_inc(s_done, 1)

                scores(0)
                for t in range(19):
                    if 2 <= t <= 17:
                        u = t - 2
                        pe.wait_ge(pn_done, 16 * half + u + 1)
                        if u >= 1:
                            pe.wait_ge(pte_a, 16 * half + u)
                            pe.wait_ge(pte_v, 16 * half + u)
                        for c in range(2 * NG):
                            ins = pe.transpose(ps[:, 4 * BANK + c * P:4 * BANK + c * P + P],
                                               SB[:, u % 3, c * P:c * P + P], ident)
                        ins.then_inc(pt_done, 1)
                    if t < 15:
                        scores(t + 1)
                    if t == 0:
                        column_sums(3 * half + 3)
                    if t == 18:
                        pe.wait_ge(o_done, 4 * half + 3)
                        column_sums(3 * half + 4, 6)
                    if t >= 3:
                        u, j, tt = t - 3, (t - 3) // 2, (t - 3) % 2
                        r, jp = 64 * (j % 2), j // 2
                        pe.wait_ge(pte_a, 16 * half + u + 1)
                        pe.wait_ge(pte_v, 16 * half + u + 1)
                        if u % 4 == 0 and jp >= 2:
                            pe.wait_ge(o_done, 4 * half + jp - 1)
                        if u == 4:
                            pe.wait_ge(mcol_done, 3 * half + 4)
                        for c in range(2 * NG):
                            ins = pe.matmul(ps[r:r + DH, (6 + jp % 2) * BANK + tt * P:(6 + jp % 2) * BANK + tt * P + P],
                                            V0[:, c % 2, c // 2, j * DH:j * DH + DH], PT[:, u % 2, c * P:c * P + P],
                                            start=(c == 0), stop=(c == 2 * NG - 1))
                        ins.then_inc(pv_done, 1)

            def mixer_out(k, m, sub):
                for j in range(4):
                    pe.wait_ge(alo_done, 4 * k + j + 1)
                    ready(m + j)
                    if j == 3:
                        spread_gate(sub)
                    for tt in range(NT):
                        for n in range(2):
                            for kk in range(2):
                                kc = 2 * j + kk
                                ins = products(bank(2 * tt + n), act_T(kc, tt * P, tt * P + P),
                                               weights(m + j, kk * D + n * BANK, kk * D + n * BANK + BANK),
                                               kc == 0, kc == KC - 1)
                        if j == 3 and tt == 0:
                            ins.then_inc(first_out, 1)
                    ins.then_inc(w_used, 1)

            mixer_out(1, M_WO0, 0)
            transpose_stream(1, lambda: pe.wait_ge(xn_done, 4))

            def open_banks(n):
                for b in range(n):
                    pe.matmul(bank(b), zb[:, 0:P], zb[:, :], start=True, stop=False, skip_group_check=True)

            def hidden_T(f, dense):
                pe.wait_ge(h_ready, f + 1)
                for fc in range(4):
                    at = (fc % 2 * 256 + fc // 2 * P) if dense else fc * P
                    ins = pe.transpose(bank(6, fc * P, fc * P + P), hsb[:, at:at + P], ident)
                ins.then_inc(t_done, 1)

            def down_tile(f, s, rr, fc0, dense, last=False):
                if fc0 == 0:
                    pe.wait_ge(hlo_done, f + 1)
                ready(s, rr)
                for tt in range(NT if dense else 1):
                    for n in range(2):
                        for k in range(2):
                            fc = (2 * k + tt) if dense else fc0 + k
                            ins = products(bank(2 * tt + n), (hhi[:, fc * P:fc * P + P], hlo[:, fc * P:fc * P + P]),
                                           weights(s, k * D + n * BANK, k * D + n * BANK + BANK), False, last and k == 1)
                    if dense and last and tt == 0:
                        ins.then_inc(first_out, 1)
                ins.then_inc(w_used, 1)

            def dense_step(f, s, rr, V=None):
                pe.wait_ge(silu_done, f)
                tokens_by_columns(4, s, rr)
                hidden_T(f - 1, True)
                tokens_by_columns(5, s + 1, rr)
                if V is not None:
                    column_sums(V)
                down_tile(f - 1, s + 2, rr, 0, True)

            pe.wait_ge(zeroed, 1)
            pe.wait_ge(x_new, 2)
            open_banks(4)
            pe.wait_ge(htv_done, 4)
            tokens_by_columns(4, M_FFN, 0, 2)
            tokens_by_columns(5, M_FFN + 1)
            with pe.Fori(0, (NHALF - 2) // 4) as i:
                for k in range(4):
                    dense_step(4 * i + k + 1, M_FFN + 2 + 3 * k, 2 * i, V_FFN + i if k == 3 else None)
            dense_step(NHALF - 1, M_FFN + 3 * NHALF - 4, 0)
            hidden_T(NHALF - 1, True)
            spread_gate(1)
            down_tile(NHALF - 1, M_IN1 - 1, 0, 0, True, last=True)
            transpose_stream(2, lambda: pe.wait_ge(xn_done, 6))

            for k in range(N_IN1):
                if k >= 2:
                    pe.wait_ge(in1_evac, k - 1)
                tokens_by_columns(k % 2, M_IN1 + k, 0, 3 if k == 0 else None)
            pe.wait_ge(rope, ROPE_END)
            for q in range(6):
                if q >= 2:
                    pe.wait_ge(q1_evac, q - 1)
                for j in range(2):
                    i = 2 * q + j
                    for tt in range(NT):
                        ins = pe.transpose(bank(4 + q % 2, (2 * j + tt) * P, (2 * j + tt + 1) * P),
                                           t1[:, tt, i * P:i * P + P], ident)
                ins.then_inc(pt_done, 1)
            def scores(u):
                i, tt = u // 2, u % 2
                if u == 0:
                    pe.wait_ge(q1_evac, 6)
                if u >= 2:
                    pe.wait_ge(e_done, 32 + u - 1)
                for r in range(2):
                    ins = pe.matmul(bank(2 * (u % 2) + r, 0, T), QT1[64 * r:64 * r + 64, i, tt * P:tt * P + P],
                                    KT1[64 * r:64 * r + 64, i // 2, :], start=True, stop=True)
                ins.then_inc(s_done, 1)

            scores(0)
            for t in range(19):
                if 2 <= t <= 17:
                    u = t - 2
                    pe.wait_ge(pn_done, 32 + u + 1)
                    if u >= 2:
                        pe.wait_ge(pte_v, 32 + u - 1)
                    for c in range(4):
                        ins = pe.transpose(bank(4 + u % 2, c * P, c * P + P), P1[:, u % 3, c * P:c * P + P], ident)
                    ins.then_inc(pt_done, 1)
                if t < 15:
                    scores(t + 1)
                if t == 18:
                    pe.wait_ge(o_done, 8 + 7)
                    column_sums(11, 6)
                if t >= 3:
                    u, i, tt = t - 3, (t - 3) // 2, (t - 3) % 2
                    pe.wait_ge(pte_v, 32 + u + 1)
                    if tt == 0 and i >= 2:
                        pe.wait_ge(o_done, 8 + i - 1)
                    for r in range(2):
                        for tk in range(NT):
                            at = D + NKV * DH + i // 2 * DH
                            ins = pe.matmul(ps[64 * r:64 * r + DH, (6 + i % 2) * BANK + tt * P:
                                               (6 + i % 2) * BANK + tt * P + P],
                                            qkv[:, tk, at:at + DH], PT1[:, u % 2, (2 * r + tk) * P:(2 * r + tk + 1) * P],
                                            start=(tk == 0), stop=(tk == 1))
                    ins.then_inc(pv_done, 1)
            mixer_out(4, M_WO1, 2)

            def logits_part(q):
                for kc in (2 * q, 2 * q + 1):
                    for tt in range(NT):
                        ins = pe.matmul(bank(6 + tt, 0, NE), ht[:, kc, tt * P:tt * P + P], rw[:, kc, :],
                                        start=(kc == 0), stop=(kc == KC - 1))
                return ins

            transpose_stream(3, lambda: pe.wait_ge(xn_done, 8), logits_part)
            pe.wait_ge(htv_done, 7)
            logits_part(2)
            pe.wait_ge(htv_done, 8)
            logits_part(3).then_inc(logits, 1)
            pe.wait_ge(route, R_CHOSEN)
            mask = [rt[:, R["mask"] + tt * NE:R["mask"] + tt * NE + NE] for tt in range(NT)]
            for at, first, second in ((0, ones, ones), (NE, upper, None), (2 * NE, ones, upper)):
                pe.matmul(bank(5, at, at + NE), first, mask[0], start=True, stop=second is None)
                if second is not None:
                    ins = pe.matmul(bank(5, at, at + NE), second, mask[1], start=False, stop=True)
            ins.then_inc(counted, 1)

            def gather(p):
                pe.wait_ge(sel_done, p + 1)
                for kc in range(KC):
                    for tt in range(NT):
                        ins = pe.matmul(ps[:, 2 * BANK + kc * P:2 * BANK + (kc + 1) * P], xo[:, tt, kc * P:(kc + 1) * P],
                                        Sel[:, tt, :], start=(tt == 0), stop=(tt == 1))
                    if kc % 4 == 3:
                        ins.then_inc(gath, 1)

            def expert_tiles(b, s, rr):
                for k in range(2):
                    ready(s + k, rr)
                    for kk in range(4):
                        kc = 4 * k + kk
                        ins = products(bank(b), act_T(kc, 0, P), weights(s + k, kk * BANK, kk * BANK + BANK),
                                       kc == 0, kc == KC - 1)
                    ins.then_inc(w_used, 1)

            def scatter(p):
                pe.wait_ge(ye_done, p + 1)
                pe.wait_ge(selT_e, p + 1)
                for n in range(4):
                    pe.matmul(bank(SCATTER_BANKS[n]), SgT[:, n // 2 * P:n // 2 * P + P],
                              ye[:, n % 2 * BANK:n % 2 * BANK + BANK], start=True, stop=True).then_inc(scat, 1)

            gather(0)
            pe.wait_ge(routed, 1)
            npass = pe.value_load(ids[0:1, NPASS + 1:NPASS + 2], min_val=NE, max_val=NPASS)
            with pe.Fori(0, npass) as p:
                rr = NF * p
                f = NHALF + NF * p
                pe.wait_ge(alo_done, 20 + p + 1)
                pe.wait_ge(silu_done, f)
                pe.wait_ge(selT_e, p + 1)
                expert_tiles(4, M_MOE, rr)
                pe.wait_ge(h_ready, f)
                pe.wait_ge(y_add, 4 * p + 1)
                expert_tiles(5, M_MOE + 2, rr)
                gather(p + 1)
                pe.wait_ge(ye_done, p + 1)
                open_banks(2)
                with pe.Fori(1, NF) as i:
                    pe.wait_ge(silu_done, f + i)
                    expert_tiles(4, M_MOE + 4, rr + i - 1)
                    hidden_T(f + i - 1, False)
                    expert_tiles(5, M_MOE + 6, rr + i - 1)
                    down_tile(f + i - 1, M_MOE + 8, rr + i - 1, 0, False)
                    down_tile(f + i - 1, M_MOE + 9, rr + i - 1, 2, False)
                hidden_T(f + NF - 1, False)
                scatter(p)
                pe.wait_ge(sg_done, p + 1)
                for tt in range(NT):
                    ins = pe.transpose(bank(4, tt * P, tt * P + P), Sg[:, tt, :], ident)
                ins.then_inc(selT, 1)
                down_tile(f + NF - 1, M_MOE + N_PASS - 2, rr, 0, False)
                down_tile(f + NF - 1, M_MOE + N_PASS - 1, rr, 2, False, last=True)
            pe.wait_ge(y_add, 4 * npass + 1)
            pe.wait_ge(selT_e, npass + 1)
            spread_gate(3)
            pe.wait_ge(gb_done, 4)
            scatter(npass)

        @block.vector
        def _(dve):
            def low(s, rr=0):
                dve.wait_ge(hi_done, s + 1 + 6 * rr)
                waits(dve, w_used, s - SPL + 1 + 6 * rr)
                dve.tensor_tensor(wlo[s % SPL][:, :], raw[s % RAW][:, :], whi[s % SPL][:, :].bitcast(F32),
                                  ALU.subtract).then_inc(lo_done, 1)

            def mod_tile(V, kc):
                dve.wait_ge(mod_landed[kc % MRAW], 16 * (2 * V + kc // MRAW + 1))
                src, c = mraw[kc % MRAW][:, :], ccol[:, kc:kc + 1]
                if kc == 0:
                    waits(dve, colsum, V)
                    dve.tensor_scalar(acc[:, :], src, c, None, ALU.mult).then_inc(mod_used, 1)
                else:
                    dve.wait_ge(mod_used, 8 * V + kc)
                    dve.scalar_tensor_tensor(acc[:, :], src, c, acc[:, :], ALU.mult, ALU.add).then_inc(mod_used, 1)

            def mod_store(V, b=7):
                dve.wait_ge(colsum, V + 1)
                dve.tensor_tensor(mcol[:, bass.ds(V, 1), :].rearrange("p a k -> p (a k)"), bank(b, 0, KC),
                                  bcol[:, bass.ds(V * KC, KC)], ALU.add).then_inc(mcol_done, 1)

            def root(c):
                dve.wait_ge(sq_done, 2 * (c + 1))
                dve.tensor_scalar(rms[:, c, :], ss[:, c, :], 1.0 / D, EPS, ALU.mult, ALU.add).then_inc(rs_done, 1)
                dve.wait_ge(sqrt_done, c + 1)
                dve.reciprocal(rstd[:, c, :], rstd[:, c, :]).then_inc(rs_done, 1)
                dve.wait_ge(rs_done, 2 * c + 2)

            def modulation(k):
                dve.wait_ge(mcol_done, k // 2 * 6 + k % 2 * 3 + 2)
                dve.scalar_tensor_tensor(acol[:, k, :], scale_of(k), 1.0, norm_of(k, 0), ALU.add,
                                         ALU.mult).then_inc(acol_done, 1)

            def normalise(c, n):
                root(c)
                for tt in range(NT):
                    dve.tensor_scalar(xo[:, tt, :], xs[:, tt, :], rstd[:, c, tt:tt + 1], None,
                                      ALU.mult).then_inc(xn_done, 1)

            def modulated(k):
                dve.wait_ge(acol_done, k + 1)
                for q in (2, 3):
                    dve.wait_ge(xT_done, 4 * k + q + 1)
                    for j in range(2):
                        kc = 2 * q + j
                        ins = dve.tensor_scalar(ht[:, kc, :], bank(4 + q % 2, j * T, j * T + T),
                                                acol[:, k, kc:kc + 1], shift_of(k)[:, kc:kc + 1], ALU.mult, ALU.add)
                    ins.then_inc(htv_done, 1)

            def low_stationary(k):
                for q in range(4):
                    dve.wait_ge(ahi_done, 4 * k + q + 1)
                    dve.tensor_tensor(alo[:, 2 * q:2 * q + 2, :], ht[:, 2 * q:2 * q + 2, :],
                                      ahi[:, 2 * q:2 * q + 2, :].bitcast(F32), ALU.subtract).then_inc(alo_done, 1)

            def diagonals(sub):
                dve.wait_ge(mcol_done, sub // 2 * 6 + sub % 2 * 3 + 3)
                dve.tensor_tensor(gcol[:, sub, :], gate_of(sub), norm_of(sub, 1), ALU.mult).then_inc(gcol_done, 1)
                dve.wait_ge(gcol_done, sub + 1)
                for kc in range(KC):
                    ins = dve.tensor_scalar(dg[:, kc * P:(kc + 1) * P], ident, gcol[:, sub, kc:kc + 1], None, ALU.mult)
                ins.then_inc(dg_done, 1)

            def residual(c, sub, ys):
                root(c)
                dve.wait_ge(gb_done, sub + 1)
                for tt in range(NT):
                    dve.scalar_tensor_tensor(xo[:, tt, :], ys[tt], rstd[:, c, tt:tt + 1], gb[:, :], ALU.mult,
                                             ALU.mult).then_inc(post_t, 1)
                for tt in range(NT):
                    dve.wait_ge(post_t, 2 * sub + tt + 1)
                    dve.tensor_tensor(xs[:, tt, :], xs[:, tt, :], xo[:, tt, :], ALU.add).then_inc(x_new, 1)

            y_banks = [ps[:, 2 * tt * BANK:2 * (tt + 1) * BANK] for tt in range(NT)]

            dve.memset(zb[:, :], 0.0).then_inc(zeroed, 1)
            dve.wait_ge(turned, 1)
            dve.tensor_copy(vcol[:, :], bank(4, 0, 72))
            dve.tensor_copy(bcol[:, :], bank(4, 128, 224)).then_inc(cols, 1)
            dve.wait_ge(cols, 1)
            dve.wait_ge(c_act, 1)
            for V in range(2):
                for kc in range(KC):
                    mod_tile(V, kc)
                if V == 0:
                    normalise(0, 0)
                mod_store(V)
            modulation(0)
            low(0)
            modulated(0)
            low_stationary(0)
            for s in range(1, SPL):
                low(s)

            with dve.Fori(0, 2) as half:
                for k in range(N_QKV_HALF):
                    low(k + SPL, 3 * half)
                    if 1 <= k <= 8:
                        mod_tile(3 * half + 2, k - 1)
                    if k == 10:
                        mod_store(3 * half + 2)
                    if k >= 10:
                        mod_tile(3 * half + 3, k - 10)
                dve.wait_ge(dist_landed, 16)
                dve.tensor_scalar(cst[:, C_DIST:NCONST], cst[:, C_DIST:NCONST], 1.0 / 16, None,
                                  ALU.mult).then_inc(dist_ok, 1)
                dve.wait_ge(dist_ok, half + 1)
                for t in range(19):
                    if t < 16:
                        u, j, tt = t, t // 2, t % 2
                        dve.wait_ge(s_done, 16 * half + u + 1)
                        if u >= 3:
                            dve.wait_ge(pt_done, 16 * half + u - 2)
                        at = C_DIST + tt * NG * T
                        dve.scalar_tensor_tensor(SB[:, u % 3, :], cst[:, at:at + NG * T], -slope(j),
                                                 ps[:, 2 * (u % 2) * BANK:2 * (u % 2) * BANK + NG * T],
                                                 ALU.mult, ALU.add).then_inc(sb_done, 1)
                        dve.wait_ge(sb_done, 16 * half + u + 1)
                        dve.tensor_reduce(nm[:, u:u + 1], SB[:, u % 3, :], AX, ALU.max, negate=True).then_inc(nm_done, 1)
                    if t == 1:
                        mod_store(3 * half + 3)
                    if 1 <= t <= 16:
                        u = t - 1
                        dve.wait_ge(e_done, 16 * half + u + 1)
                        dve.reciprocal(rden[:, u:u + 1], den[:, u:u + 1]).then_inc(rd_done, 1)
                        dve.wait_ge(rd_done, 16 * half + u + 1)
                        dve.tensor_scalar(SB[:, u % 3, :], SB[:, u % 3, :], rden[:, u:u + 1], None,
                                          ALU.mult).then_inc(pn_done, 1)
                    if 2 <= t <= 17:
                        u = t - 2
                        dve.wait_ge(pt_done, 16 * half + u + 1)
                        dve.tensor_copy(PT[:, u % 2, BANK:NG * T], bank(5, 0, NG * T - BANK)).then_inc(pte_v, 1)
                    if 1 <= t <= 15 and t % 2:
                        mod_tile(3 * half + 4, t // 2)
                mod_store(3 * half + 4, 6)

            def mixer_out(k, m, c, sub):
                for q in range(4):
                    dve.wait_ge(ahi_done, 4 * k + q + 1)
                    dve.tensor_tensor(alo[:, 2 * q:2 * q + 2, :], oT[:, 2 * q:2 * q + 2, :],
                                      ahi[:, 2 * q:2 * q + 2, :].bitcast(F32), ALU.subtract).then_inc(alo_done, 1)
                diagonals(sub)
                for j in range(3):
                    low(m + j + SPL)
                residual(c, sub, y_banks)

            mixer_out(1, M_WO0, 1, 0)
            modulation(1)
            dve.wait_ge(x_new, 2)
            normalise(2, 1)
            low(M_WO0 + 3 + SPL)
            modulated(1)
            low_stationary(2)
            diagonals(1)

            def hidden(f, used):
                dve.wait_ge(silu_done, f + 1)
                dve.wait_ge(w_used, used)
                dve.tensor_tensor(hsb, sgl, bank(5), ALU.mult).then_inc(h_ready, 1)

            def hidden_low(f):
                dve.wait_ge(hhi_done, f + 1)
                dve.tensor_tensor(hlo[:, :], bank(6), hhi[:, :].bitcast(F32), ALU.subtract).then_inc(hlo_done, 1)

            def dense_step(f, s, rr, between=()):
                low(s + SPL, rr)
                hidden_low(f - 1)
                if len(between) > 2:
                    between[0]()
                hidden(f, s + 2 + 6 * rr)
                low(s + 1 + SPL, rr)
                if len(between) > 1:
                    between[-2]()
                low(s + 2 + SPL, rr)
                if between:
                    between[-1]()

            low(M_FFN + SPL)
            hidden(0, M_FFN + 2)
            low(M_FFN + 1 + SPL)
            with dve.Fori(0, (NHALF - 2) // 4) as i:
                for k in range(4):
                    dense_step(4 * i + k + 1, M_FFN + 2 + 3 * k, 2 * i,
                               [lambda kc=kc: mod_tile(V_FFN + i, kc) for kc in range(3 * k, min(3 * k + 3, KC))])
                mod_store(V_FFN + i)
            dense_step(NHALF - 1, M_FFN + 3 * NHALF - 4, 0)
            hidden_low(NHALF - 1)
            residual(3, 1, y_banks)
            modulation(2)
            dve.wait_ge(x_new, 4)
            normalise(4, 2)
            low(M_IN1 - 1 + SPL)
            modulated(2)
            low_stationary(3)

            step = [0]

            def chain(ins):
                step[0] += 1
                ins.then_inc(rope, 1)
                dve.wait_ge(rope, step[0])

            for tt in range(NT):
                for n in range(2):
                    g = gq[:, n, :].rearrange("p (b c d) -> p b c d", b=2, c=2)
                    sn = cst[:, C_SIN + tt * DH:C_SIN + tt * DH + DH].rearrange("p (b c d) -> p b c d", b=2, c=2)
                    so = sg_[:, tt, n, :].rearrange("p (b c d) -> p b c d", b=2, c=2)
                    dve.tensor_tensor(cg[:, tt, n, :], gq[:, n, :], cst[:, C_COS + tt * DH:C_COS + tt * DH + DH], ALU.mult)
                    for c in range(2):
                        ins = dve.tensor_tensor(so[:, :, c, :], g[:, :, 1 - c, :], sn[:, :, c, :], ALU.mult)
            chain(ins)
            for k in range(N_IN1):
                if k < 5:
                    qk = qkv[:, :, k * 256:k * 256 + 256].rearrange("p t (h d) -> p t h d", d=DH)
                    n, q4 = k // 4, DH // 4
                    dve.wait_ge(in1_evac, k + 1)
                    chain(dve.tensor_reduce(hs1[:, 2, k], t2[:, 0], AX, ALU.add))
                    chain(dve.tensor_scalar(hs1[:, 1, k], hs1[:, 2, k], 1.0 / DH, EPS, ALU.mult, ALU.add))
                low(M_IN1 + k + SPL)
                if k < 5:
                    dve.wait_ge(hroot, k + 1)
                    chain(dve.reciprocal(hs1[:, 2, k], hs1[:, 0, k]))
                    chain(dve.tensor_tensor(qk, qk, hs1[:, 2, k].unsqueeze(3).broadcast_to([P, NT, 4, DH]), ALU.mult))
                    for b in range(2):
                        for c in range(2):
                            at, frm = (2 * b + c) * q4, (2 * b + 1 - c) * q4
                            ins = dve.tensor_tensor(
                                t2[:, 1, :, :, at:at + q4], qk[:, :, :, frm:frm + q4],
                                sg_[:, :, n, at:at + q4].unsqueeze(2).broadcast_to([P, NT, 4, q4]), ALU.mult)
                    chain(ins)
                    chain(dve.tensor_tensor(qk, qk, cg[:, :, n, :].unsqueeze(2).broadcast_to([P, NT, 4, DH]), ALU.mult))
                    if n == 0:
                        dst = t1[:, :, k * 256:k * 256 + 256].rearrange("p t (h d) -> p t h d", d=DH)
                        chain(dve.tensor_tensor(dst, qk, t2[:, 1], ALU.add))
                    else:
                        dst = t1[:, :, D:D + 2 * NKV * DH].rearrange("p t (h c d) -> p t h c d", h=NKV, c=2)
                        for c in range(2):
                            ins = dve.tensor_tensor(dst[:, :, :, c, :], qk, t2[:, 1], ALU.add)
                        chain(ins)
            assert step[0] == ROPE_END, step

            for t in range(19):
                if t < 16:
                    u = t
                    dve.wait_ge(s_done, 32 + u + 1)
                    src = ps[:, 2 * (u % 2) * BANK:2 * (u % 2) * BANK + 2 * BANK].rearrange("p (r c) -> p r c", r=2)
                    dve.tensor_reduce(nm[:, 2 * u:2 * u + 2], src[:, :, 0:T], AX, ALU.max, negate=True).then_inc(nm_done, 1)
                if 1 <= t <= 16:
                    u = t - 1
                    dve.wait_ge(e_done, 32 + u + 1)
                    dve.reciprocal(rden[:, 2 * u:2 * u + 2], den[:, 2 * u:2 * u + 2]).then_inc(rd_done, 1)
                    dve.wait_ge(rd_done, 32 + u + 1)
                    for r in range(2):
                        pr = P1[:, u % 3, r * T:r * T + T]
                        ins = dve.tensor_scalar(pr, pr, rden[:, 2 * u + r:2 * u + r + 1], None, ALU.mult)
                    ins.then_inc(pn_done, 1)
                if 2 <= t <= 17:
                    u = t - 2
                    dve.wait_ge(pt_done, 38 + u + 1)
                    dve.tensor_copy(PT1[:, u % 2, :], bank(4 + u % 2)).then_inc(pte_v, 1)
                if 1 <= t <= 15 and t % 2:
                    mod_tile(11, t // 2)
            mod_store(11, 6)
            dve.memset(ye, 0.0).then_inc(ye_done, 1)
            dve.memset(SgT, 0.0).then_inc(selT_e, 1)
            mixer_out(4, M_WO1, 5, 2)
            modulation(3)
            dve.wait_ge(x_new, 6)
            normalise(6, 3)
            low(M_WO1 + 3 + SPL)
            modulated(3)

            def slots(v):
                for tt in range(NT):
                    ins = dve.tensor_scalar(Sel[:, tt, :], iota, v[tt], None, ALU.is_equal)
                ins.then_inc(sel_done, 1)

            made = [0]

            def routing(ins):
                made[0] += 1
                ins.then_inc(route, 1)
                dve.wait_ge(route, made[0])

            def r3(name):
                return rt[:, R[name]:R[name] + 16].rearrange("p (t e) -> p t e", t=NT)

            def per_tile(at):
                return rt[:, at:at + 2]

            def spread(v):
                return v.unsqueeze(2).broadcast_to([P, NT, NE])

            def over_tiles(v):
                return v.unsqueeze(1).broadcast_to([P, NT, NE])

            desc = cst[:, C_DESC:C_DESC + NE]
            dve.wait_ge(logits, 1)
            routing(dve.tensor_copy(r3("L"), ps[:, 6 * BANK:8 * BANK].rearrange("p (t c) -> p t c", t=NT)[:, :, 0:NE]))
            for src, mx, fx, oh in (("L", R_M1, R_F, "oh1"), ("l2", R_M2, R_F2, "oh2")):
                routing(dve.tensor_reduce(per_tile(mx), r3(src), AX, ALU.max))
                routing(dve.tensor_tensor(r3("eq"), r3(src), spread(per_tile(mx)), ALU.is_equal))
                routing(dve.tensor_tensor(r3("cand"), r3("eq"), over_tiles(desc), ALU.mult))
                routing(dve.tensor_reduce(per_tile(fx), r3("cand"), AX, ALU.max))
                routing(dve.tensor_tensor(r3(oh), over_tiles(desc), spread(per_tile(fx)), ALU.is_equal))
                if oh == "oh1":
                    routing(dve.scalar_tensor_tensor(rt[:, R["l2"]:R["l2"] + 16], rt[:, R["oh1"]:R["oh1"] + 16], -BIG,
                                                     rt[:, R["L"]:R["L"] + 16], ALU.mult, ALU.add))
            routing(dve.tensor_tensor(r3("mask"), r3("oh1"), r3("oh2"), ALU.add))
            assert made[0] == R_CHOSEN
            routing(dve.tensor_tensor(per_tile(R_D), per_tile(R_M2), per_tile(R_M1), ALU.subtract))
            assert made[0] == R_DIFF
            dve.wait_ge(counted, 1)
            routing(dve.scalar_tensor_tensor(rt[:, R["rank"]:R["rank"] + 16], bank(5, NE, 3 * NE), 1.0,
                                             rt[:, R["mask"]:R["mask"] + 16], ALU.add, ALU.mult))
            routing(dve.tensor_scalar(rt[:, R["rank"]:R["rank"] + 16], rt[:, R["rank"]:R["rank"] + 16], -1.0, None, ALU.add))
            slots([rt[:, R["rank"] + tt * NE:R["rank"] + tt * NE + 1] for tt in range(NT)])
            dve.wait_ge(e_gate, 1)
            routing(dve.tensor_scalar(per_tile(R_G2), per_tile(R_E), 1.0, None, ALU.add))
            routing(dve.reciprocal(per_tile(R_G1), per_tile(R_G2)))
            routing(dve.tensor_tensor(per_tile(R_G2), per_tile(R_E), per_tile(R_G1), ALU.mult))
            routing(dve.tensor_tensor(r3("gate"), r3("oh1"), spread(per_tile(R_G1)), ALU.mult))
            routing(dve.tensor_tensor(r3("gt2"), r3("oh2"), spread(per_tile(R_G2)), ALU.mult))
            routing(dve.tensor_tensor(r3("gate"), r3("gate"), r3("gt2"), ALU.add))
            ovf, cum = rt[:, R_OVF:R_OVF + NE], rt[:, R_CUM:R_CUM + NE]
            other = rt[:, R_CUM + NE:R_CUM + 2 * NE]
            routing(dve.tensor_scalar(ovf, bank(5, 0, NE), float(P), None, ALU.is_gt))
            a, b = ovf, cum
            for d in (1, 2, 4):
                routing(dve.tensor_copy(b, a))
                routing(dve.tensor_tensor(b[:, d:NE], a[:, d:NE], a[:, 0:NE - d], ALU.add))
                a, b = b, (other if b is cum else cum)
            total = a[:, NE - 1:NE]
            routing(dve.tensor_scalar(idf[:, NPASS + 1:NPASS + 2], total, float(NE), None, ALU.add))
            routing(dve.tensor_tensor(b, a, ovf, ALU.subtract))
            before = b
            routing(dve.memset(tab[:, :, :], -1.0))
            routing(dve.memset(idf[:, NPASS:NPASS + 1], 0.0))
            routing(dve.tensor_copy(idf[:, 0:NE], cst[:, C_EI:C_EI + NE]))
            for name, at in (("rank", 0), ("gate", 2)):
                routing(dve.tensor_copy(tab[:, 0:NE, at:at + 2].rearrange("p e t -> p t e"), r3(name)))
            sel = rt[:, R["eq"]:R["eq"] + NE]
            for x in range(NEXTRA):
                routing(dve.scalar_tensor_tensor(sel, before, float(x), ovf, ALU.is_equal, ALU.mult))
                routing(dve.tensor_tensor(rt[:, R["cand"]:R["cand"] + NE], sel, cst[:, C_EI:C_EI + NE], ALU.mult))
                routing(dve.tensor_reduce(idf[:, NE + x:NE + x + 1], rt[:, R["cand"]:R["cand"] + NE], AX, ALU.add))
                for name, at in (("rank", 0), ("gate", 2)):
                    routing(dve.tensor_tensor(r3("tmp"), r3(name), over_tiles(sel), ALU.mult))
                    if at:
                        routing(dve.tensor_reduce(tab[:, NE + x, at:at + 2], r3("tmp"), AX, ALU.add))
                    else:
                        routing(dve.tensor_reduce(per_tile(R_F), r3("tmp"), AX, ALU.add))
                        routing(dve.tensor_scalar(tab[:, NE + x, 0:2], per_tile(R_F), -float(P), None, ALU.add))
            dve.tensor_copy(ids[0:1, 0:NPASS + 2], idf[0:1, 0:NPASS + 2]).then_inc(routed, 1)
            dve.wait_ge(routed, 1)
            npass = dve.value_load(ids[0:1, NPASS + 1:NPASS + 2], min_val=NE, max_val=NPASS)

            def add_scattered(p):
                dve.wait_ge(y_add, 1 + 4 * p)
                for n in range(4):
                    dve.wait_ge(scat, 4 * p + n + 1)
                    part = yacc[:, n // 2, n % 2 * BANK:n % 2 * BANK + BANK]
                    dve.tensor_tensor(part, part, bank(SCATTER_BANKS[n]), ALU.add).then_inc(y_add, 1)

            def gathered_low(p):
                dve.wait_ge(ahi_done, 20 + p + 1)
                dve.tensor_tensor(alo[:, :, 0:P], xg, ahi[:, :, 0:P].bitcast(F32), ALU.subtract).then_inc(alo_done, 1)

            gathered_low(0)
            dve.memset(yacc, 0.0).then_inc(y_add, 1)
            diagonals(3)
            with dve.Fori(0, npass) as p:
                rr = NF * p
                f = NHALF + NF * p
                dve.tensor_copy(cur[:, :], tab[:, bass.ds(p, 2), :].rearrange("p a c -> p (a c)")).then_inc(cur_done, 1)
                dve.wait_ge(cur_done, p + 1)
                for tt in range(NT):
                    ins = dve.tensor_scalar(Sg[:, tt, :], iota, cur[:, tt:tt + 1], cur[:, 2 + tt:3 + tt],
                                            ALU.is_equal, ALU.mult)
                ins.then_inc(sg_done, 1)
                slots([cur[:, 4 + tt:5 + tt] for tt in range(NT)])
                for k in range(3):
                    low(M_MOE + k + SPL, rr)
                hidden(f, M_MOE + 4 + 6 * rr)
                low(M_MOE + 3 + SPL, rr)
                with dve.Fori(1, NF) as i:
                    s, q = M_MOE + 4, rr + i - 1
                    low(s + SPL, q)
                    low(s + 1 + SPL, q)
                    hidden_low(f + i - 1)
                    low(s + 2 + SPL, q)
                    hidden(f + i, s + 4 + 6 * q)
                    for k in range(3, 6):
                        low(s + k + SPL, q)
                hidden_low(f + NF - 1)
                dve.wait_ge(selT, p + 1)
                dve.tensor_copy(SgT, bank(4, 0, NT * P)).then_inc(selT_e, 1)
                gathered_low(p + 1)
                add_scattered(p)
                for k in range(2):
                    low(M_MOE + N_PASS - 2 + k + SPL, rr)
            add_scattered(npass)
            residual(7, 3, [yacc[:, tt, :] for tt in range(NT)])


_INS = ["x", "c", "mod_w", "mod_b", "norm_g", "l0_w_in", "l0_w_out", "l0_ffn_w_gate", "l0_ffn_w_up", "l0_ffn_w_down",
        "l1_w_in", "l1_q_norm_g", "l1_k_norm_g", "l1_w_out", "l1_router_w", "l1_exp_w_gate", "l1_exp_w_up",
        "l1_exp_w_down"]


def kernel(**inputs):
    import concourse.bacc as bacc
    from concourse.bass_utils import run_bass_kernel_spmd

    nc = bacc.Bacc("TRN2", target_bir_lowering=False, num_devices=1, dynamic_dma_scratch_size=DGE_RING)
    arrays = {name: np.ascontiguousarray(inputs[name]) for name in _INS}
    arrays["consts"] = constants()
    dram = {name: nc.dram_tensor(name, a.shape, mybir.dt.from_np(a.dtype), kind="ExternalInput").ap()
            for name, a in arrays.items()}
    out = nc.dram_tensor("out", (1, T, D), F32, kind="ExternalOutput").ap()
    build(nc, dram, out)
    r = run_bass_kernel_spmd(nc, [arrays], core_ids=[0])
    return r.results[0]["out"]
```
